# Optimizing a Trainium2 kernel written in Bass

```python
import jax, jax.numpy as jnp
from jax import lax
import numpy as np

D_MODEL = 1024
BATCH = 1
SEQ = 128
DEPTH = 1
DEC_BATCH = 1
DEC_SEQ = 512
PAST_LEN = 128

GRID_W = 64
HEAD_DIM = 64
A_HEADS = 8
A_KV_HEADS = 2
A_WINDOW = 128
A_BLOCK = 128
B_HEADS = 8
NA_ROWS = 8
NA_COLS = 16
D_FF = -(-8 * D_MODEL // (3 * 256)) * 256
ROPE_BASE = 10000.0
RMS_EPS = 1e-6
NEG = -1e30

A_Q = A_HEADS * HEAD_DIM
A_KV = A_KV_HEADS * HEAD_DIM
B_W = B_HEADS * HEAD_DIM
D_IN = A_Q + 2 * A_KV + 3 * B_W + 2 * D_MODEL
SPLITS = [A_Q, A_Q + A_KV, A_Q + 2 * A_KV, A_Q + 2 * A_KV + B_W,
          A_Q + 2 * A_KV + 2 * B_W, A_Q + 2 * A_KV + 3 * B_W,
          A_Q + 2 * A_KV + 3 * B_W + D_MODEL]

kernel_name = "hybrid_dit_window_natten_prefix_step"

def rmsnorm(x, g):
    xf = x.astype(jnp.float32)
    y = xf * lax.rsqrt(jnp.mean(xf * xf, axis=-1, keepdims=True) + RMS_EPS)
    return (y * g.astype(jnp.float32)).astype(x.dtype)

def ada_mod(cvec, w_ada_l, b_ada_l):
    m = jax.nn.silu(cvec) @ w_ada_l + b_ada_l
    return jnp.split(m, 6, axis=-1)

def modulate(h, shift, scale):
    return h * (1 + scale) + shift

def rope_axis(x, pos):
    half = x.shape[-1] // 2
    inv_freq = 1.0 / (ROPE_BASE ** (jnp.arange(half, dtype=jnp.float32) / half))
    ang = pos.astype(jnp.float32)[:, None] * inv_freq[None, :]
    cos = jnp.cos(ang)[:, None, :]
    sin = jnp.sin(ang)[:, None, :]
    xf = x.astype(jnp.float32)
    x1, x2 = xf[..., :half], xf[..., half:]
    return jnp.concatenate([x1 * cos - x2 * sin, x2 * cos + x1 * sin], axis=-1).astype(x.dtype)

def rope_2d(x):
    n = x.shape[1]
    t = jnp.arange(n)
    d2 = HEAD_DIM // 2
    return jnp.concatenate([rope_axis(x[..., :d2], t // GRID_W), rope_axis(x[..., d2:], t % GRID_W)], axis=-1)

def project(h, w_in_l, qn_a, kn_a, qn_b, kn_b):
    u = h @ w_in_l
    qa, ka, va, qb, kb, vb, ga, gb = jnp.split(u, SPLITS, axis=-1)
    lead = h.shape[:-1]
    qa = rmsnorm(qa.reshape(*lead, A_HEADS, HEAD_DIM), qn_a)
    ka = rmsnorm(ka.reshape(*lead, A_KV_HEADS, HEAD_DIM), kn_a)
    va = va.reshape(*lead, A_KV_HEADS, HEAD_DIM)
    qb = rmsnorm(qb.reshape(*lead, B_HEADS, HEAD_DIM), qn_b)
    kb = rmsnorm(kb.reshape(*lead, B_HEADS, HEAD_DIM), kn_b)
    vb = vb.reshape(*lead, B_HEADS, HEAD_DIM)
    return qa, ka, va, qb, kb, vb, ga, gb

def merge_out(ya, yb, ga, gb, w_out_a_l, w_out_b_l, w_o_l):
    return (jax.nn.sigmoid(ga) * (ya @ w_out_a_l) + jax.nn.sigmoid(gb) * (yb @ w_out_b_l)) @ w_o_l

def swiglu(h, wg, wu, wd):
    return (jax.nn.silu(h @ wg) * (h @ wu)) @ wd

def ctx_attention(q, k, v, sink):
    b, l, h, d = q.shape
    kv = k.shape[2]
    g = h // kv
    m = k.shape[1]
    qg = q.reshape(b, l, kv, g, d)
    s = jnp.einsum('blkgd,bmkd->bkglm', qg, k).astype(jnp.float32) * (d ** -0.5)
    if sink is not None:
        s_sink = jnp.broadcast_to(sink.reshape(kv, g)[None, :, :, None, None].astype(jnp.float32), (b, kv, g, l, 1))
        s = jnp.concatenate([s, s_sink], axis=-1)
    p = jax.nn.softmax(s, axis=-1)[..., :m].astype(v.dtype)
    return jnp.einsum('bkglm,bmkd->blkgd', p, v).reshape(b, l, h * d)

def window_attention(q, k, v, ck, cv, sink):
    b, n, h, d = q.shape
    kv = k.shape[2]
    g = h // kv
    nb = n // A_BLOCK
    lc = ck.shape[1]
    qb = q.reshape(b, nb, A_BLOCK, kv, g, d)
    pad = ((0, 0), (A_BLOCK, A_BLOCK), (0, 0), (0, 0))
    kp = jnp.pad(k, pad).reshape(b, nb + 2, A_BLOCK, kv, d)
    vp = jnp.pad(v, pad).reshape(b, nb + 2, A_BLOCK, kv, d)
    kb = jnp.concatenate([kp[:, :nb], kp[:, 1:nb + 1], kp[:, 2:]], axis=2)
    vb = jnp.concatenate([vp[:, :nb], vp[:, 1:nb + 1], vp[:, 2:]], axis=2)
    qpos = jnp.arange(n).reshape(nb, A_BLOCK)
    kpos = (jnp.arange(nb)[:, None] - 1) * A_BLOCK + jnp.arange(3 * A_BLOCK)[None, :]
    kq = kpos[:, None, :]
    valid = (jnp.abs(qpos[:, :, None] - kq) <= A_WINDOW) & (kq >= 0) & (kq < n)
    scale = d ** -0.5
    s_loc = jnp.einsum('bnqkgd,bnskd->bnkgqs', qb, kb).astype(jnp.float32) * scale
    s_loc = jnp.where(valid[None, :, None, None], s_loc, NEG)
    s_ctx = jnp.einsum('bnqkgd,blkd->bnkgql', qb, ck).astype(jnp.float32) * scale
    s_sink = jnp.broadcast_to(sink.reshape(kv, g)[None, None, :, :, None, None].astype(jnp.float32), (b, nb, kv, g, A_BLOCK, 1))
    p = jax.nn.softmax(jnp.concatenate([s_loc, s_ctx, s_sink], axis=-1), axis=-1)
    p_loc = p[..., :3 * A_BLOCK].astype(v.dtype)
    p_ctx = p[..., 3 * A_BLOCK:3 * A_BLOCK + lc].astype(v.dtype)
    out = jnp.einsum('bnkgqs,bnskd->bnqkgd', p_loc, vb) + jnp.einsum('bnkgql,blkd->bnqkgd', p_ctx, cv)
    return out.reshape(b, n, h * d)

def neighbourhood_attention(q, k, v, ck, cv, rpb):
    b, n, h, d = q.shape
    rows_n = n // GRID_W
    wr = min(NA_ROWS, rows_n)
    s_len = wr * GRID_W
    rq = jnp.arange(rows_n)
    rs = jnp.clip(rq - wr // 2, 0, rows_n - wr)
    rows = rs[:, None] + jnp.arange(wr)[None, :]
    kg = k.reshape(b, rows_n, GRID_W, h, d)[:, rows].reshape(b, rows_n, s_len, h, d)
    vg = v.reshape(b, rows_n, GRID_W, h, d)[:, rows].reshape(b, rows_n, s_len, h, d)
    qg = q.reshape(b, rows_n, GRID_W, h, d)
    cq = jnp.arange(GRID_W)
    cs = jnp.clip(cq - NA_COLS // 2, 0, GRID_W - NA_COLS)
    kcol = jnp.arange(s_len) % GRID_W
    krow = jnp.repeat(rows, GRID_W, axis=1)
    col_valid = (kcol[None, :] >= cs[:, None]) & (kcol[None, :] < cs[:, None] + NA_COLS)
    dr = krow - rq[:, None] + (NA_ROWS - 1)
    dc = jnp.clip(kcol[None, :] - cq[:, None], -(NA_COLS - 1), NA_COLS - 1) + (NA_COLS - 1)
    bias = jnp.transpose(rpb[:, dr[:, None, :], dc[None, :, :]], (1, 0, 2, 3))
    scale = d ** -0.5
    s_loc = jnp.einsum('brqhd,brshd->brhqs', qg, kg).astype(jnp.float32) * scale + bias.astype(jnp.float32)[None]
    s_loc = jnp.where(col_valid[None, None, None], s_loc, NEG)
    s_ctx = jnp.einsum('brqhd,blhd->brhql', qg, ck).astype(jnp.float32) * scale
    p = jax.nn.softmax(jnp.concatenate([s_loc, s_ctx], axis=-1), axis=-1)
    p_loc = p[..., :s_len].astype(v.dtype)
    p_ctx = p[..., s_len:].astype(v.dtype)
    out = jnp.einsum('brhqs,brshd->brqhd', p_loc, vg) + jnp.einsum('brhql,blhd->brqhd', p_ctx, cv)
    return out.reshape(b, n, h * d)

def setup_inputs(seed: int = 0) -> dict:
    key = jax.random.key(seed)
    ks = jax.random.split(key, 26)
    f32 = jnp.float32
    nrm = lambda k, s: jax.random.normal(k, s, dtype=f32)
    return {
        "x_prompt": nrm(ks[0], (BATCH, SEQ, D_MODEL)),
        "x_sample": nrm(ks[1], (DEC_BATCH, DEC_SEQ, D_MODEL)),
        "cache_a_k": nrm(ks[2], (DEC_BATCH, DEPTH, PAST_LEN, A_KV_HEADS, HEAD_DIM)),
        "cache_a_v": nrm(ks[3], (DEC_BATCH, DEPTH, PAST_LEN, A_KV_HEADS, HEAD_DIM)),
        "cache_b_k": nrm(ks[4], (DEC_BATCH, DEPTH, PAST_LEN, B_HEADS, HEAD_DIM)),
        "cache_b_v": nrm(ks[5], (DEC_BATCH, DEPTH, PAST_LEN, B_HEADS, HEAD_DIM)),
        "c": nrm(ks[6], (DEC_BATCH, D_MODEL)),
        "c_ctx": nrm(ks[7], (D_MODEL,)),
        "w_ada": nrm(ks[8], (DEPTH, D_MODEL, 6 * D_MODEL)) * (0.5 * D_MODEL ** -0.5),
        "b_ada": nrm(ks[9], (DEPTH, 6 * D_MODEL)) * 0.02,
        "g_attn": 1.0 + 0.05 * nrm(ks[10], (DEPTH, D_MODEL)),
        "w_in": nrm(ks[11], (DEPTH, D_MODEL, D_IN)) * D_MODEL ** -0.5,
        "q_norm_a": 1.0 + 0.05 * nrm(ks[12], (DEPTH, HEAD_DIM)),
        "k_norm_a": 1.0 + 0.05 * nrm(ks[13], (DEPTH, HEAD_DIM)),
        "q_norm_b": 1.0 + 0.05 * nrm(ks[14], (DEPTH, HEAD_DIM)),
        "k_norm_b": 1.0 + 0.05 * nrm(ks[15], (DEPTH, HEAD_DIM)),
        "sink_a": nrm(ks[16], (DEPTH, A_HEADS)),
        "rpb_b": 0.1 * nrm(ks[17], (DEPTH, B_HEADS, 2 * NA_ROWS - 1, 2 * NA_COLS - 1)),
        "w_out_a": nrm(ks[18], (DEPTH, A_Q, D_MODEL)) * A_Q ** -0.5,
        "w_out_b": nrm(ks[19], (DEPTH, B_W, D_MODEL)) * B_W ** -0.5,
        "w_o": nrm(ks[20], (DEPTH, D_MODEL, D_MODEL)) * D_MODEL ** -0.5,
        "g_ffn": 1.0 + 0.05 * nrm(ks[21], (DEPTH, D_MODEL)),
        "w_gate": nrm(ks[22], (DEPTH, D_MODEL, D_FF)) * D_MODEL ** -0.5,
        "w_up": nrm(ks[23], (DEPTH, D_MODEL, D_FF)) * D_MODEL ** -0.5,
        "w_down": nrm(ks[24], (DEPTH, D_FF, D_MODEL)) * D_FF ** -0.5,
    }

def reference(x_prompt, x_sample, cache_a_k, cache_a_v, cache_b_k, cache_b_v, c, c_ctx,
              w_ada, b_ada, g_attn, w_in, q_norm_a, k_norm_a, q_norm_b, k_norm_b,
              sink_a, rpb_b, w_out_a, w_out_b, w_o, g_ffn, w_gate, w_up, w_down):
    xp = x_prompt
    xs = x_sample
    ak_list, av_list, bk_list, bv_list = [], [], [], []
    for l in range(DEPTH):
        sh1, sc1, gt1, sh2, sc2, gt2 = ada_mod(c_ctx, w_ada[l], b_ada[l])
        h = modulate(rmsnorm(xp, g_attn[l]), sh1, sc1)
        qa, ka, va, qb, kb, vb, ga, gb = project(h, w_in[l], q_norm_a[l], k_norm_a[l], q_norm_b[l], k_norm_b[l])
        ya = ctx_attention(qa, ka, va, sink_a[l])
        yb = ctx_attention(qb, kb, vb, None)
        xp = xp + gt1 * merge_out(ya, yb, ga, gb, w_out_a[l], w_out_b[l], w_o[l])
        xp = xp + gt2 * swiglu(modulate(rmsnorm(xp, g_ffn[l]), sh2, sc2), w_gate[l], w_up[l], w_down[l])
        ak_list.append(ka)
        av_list.append(va)
        bk_list.append(kb)
        bv_list.append(vb)

        sh1, sc1, gt1, sh2, sc2, gt2 = [m[:, None, :] for m in ada_mod(c, w_ada[l], b_ada[l])]
        h = modulate(rmsnorm(xs, g_attn[l]), sh1, sc1)
        qa, ka, va, qb, kb, vb, ga, gb = project(h, w_in[l], q_norm_a[l], k_norm_a[l], q_norm_b[l], k_norm_b[l])
        qa = rope_2d(qa)
        ka = rope_2d(ka)
        ya = window_attention(qa, ka, va, cache_a_k[:, l], cache_a_v[:, l], sink_a[l])
        yb = neighbourhood_attention(qb, kb, vb, cache_b_k[:, l], cache_b_v[:, l], rpb_b[l])
        xs = xs + gt1 * merge_out(ya, yb, ga, gb, w_out_a[l], w_out_b[l], w_o[l])
        xs = xs + gt2 * swiglu(modulate(rmsnorm(xs, g_ffn[l]), sh2, sc2), w_gate[l], w_up[l], w_down[l])
    new_a_k = jnp.stack(ak_list, axis=1)
    new_a_v = jnp.stack(av_list, axis=1)
    new_b_k = jnp.stack(bk_list, axis=1)
    new_b_v = jnp.stack(bv_list, axis=1)
    return (xp, xs, new_a_k, new_a_v, new_b_k, new_b_v)


_drawn_inputs = setup_inputs


def setup_inputs(seed=0):
    import zlib

    import numpy as np

    out = dict(_drawn_inputs(seed))
    spreads = {}
    factors = {'cache_a_k': 7.559,
     'cache_a_v': 6.153,
     'cache_b_k': 5.789,
     'cache_b_v': 4.335,
     'q_norm_a': 8.0,
     'q_norm_b': 8.0,
     'sink_a': 64.0,
     'rpb_b': 8.0,
     'g_ffn': 3.932}
    for name, (base, spread) in spreads.items():
        noise = np.random.default_rng([zlib.crc32(name.encode()), seed]).standard_normal(out[name].shape)
        drawn = base * np.exp(spread * noise) if base else spread * noise
        out[name] = __import__('jax').numpy.asarray(drawn.astype(out[name].dtype))
    for name, factor in factors.items():
        out[name] = (out[name] * factor).astype(out[name].dtype)
    return out
```

```python
import numpy as np
import concourse.bass as bass
from concourse import mybir
from contextlib import ExitStack, contextmanager

P = 128
D_MODEL, D_FF = 1024, 2816
CTX, LAT = 128, 512
T = CTX + LAT
TH = T // 2
KT = D_MODEL // P
GRID_W, HD = 64, 64
ROWS = LAT // GRID_W
A_HEADS, B_HEADS = 8, 8
NA_ROWS, NA_COLS = 8, 16
NEG = -1e30
BIG = 3.0e38
RMS_EPS = 1e-6
SCALE = HD ** -0.5

B_COL0 = [0, 8, 24, 40]
B_NCOL = [24, 32, 32, 24]

RING = 4
N_QKV = 18
U_GATE = N_QKV
N_GATE = 8
N_GATE_ATT = 7
U_OUT = U_GATE + N_GATE
U_MERGE = U_OUT + 4
U_WO = U_MERGE + 12
U_FFN = U_WO + KT
FF_PARTS = [8, 8, 6]
N_UNITS = U_FFN + sum(2 * f + KT for f in FF_PARTS)
SHIFT1, SCALE1, GATE1, SHIFT2, SCALE2, GATE2 = range(6)
N_ADA1, ADA1_SLOTS = 2 * KT, 10
N_ADA2, ADA2_SLOTS = 4 * KT, 5
ADA2_OF = [1] * 4 + [2] * 9 + [0, 1, 1, 1, 0]
ADA2_QKV = sum(ADA2_OF)

V_BADA, V_GATTN, V_GFFN, V_GAIN, V_SINK, N_VEC = 0, 48, 56, 64, 68, 76
C_IDENT, C_HEADS, C_ONE, C_COS, C_SIN, C_MASK, N_CONST = 0, 128, 130, 131, 643, 1155, 1667

QA, KA, QB, KB, VA_T, VB_T = 0, 4, 5, 9, 13, 14
N_STAT = 13
STAT_COLS = 10


class Chain:

    def __init__(self, eng, sem):
        self.eng, self.sem, self.n, self.loop = eng, sem, 0, 0

    def mark(self, ins):
        ins.then_inc(self.sem, 1)
        self.n += 1

    def wait(self):
        self.eng.wait_ge(self.sem, self.n + self.loop)

    @contextmanager
    def fori(self, n, stride):
        start = self.n
        with self.eng.Fori(0, n) as i:
            self.loop = i * stride
            yield i
            assert self.n - start == stride, (self.n - start, stride)
        self.loop = 0
        self.n += (n - 1) * stride


def hybrid_dit_program(nc, x_t, c_t, c_row, w_scale1, w_ada, w_main, vecs, consts, cache_ka,
                       cache_va, cache_kb, cache_vb, rpb, y_t, new_ka, new_va, new_kb, new_vb):
    F32, F32R = mybir.dt.float32, mybir.dt.float32r
    ALU, ACT = mybir.AluOpType, mybir.ActivationFunctionType
    ds = bass.ds

    ctx = ExitStack()
    with ctx:
        def sb(name, shape, dt=F32, scope=ctx):
            return scope.enter_context(nc.sbuf_tensor(name, shape, dt))

        def sem(name):
            return ctx.enter_context(nc.semaphore(name))

        vec = sb("vec", [P, N_VEC])
        cst = sb("cst", [P, C_COS])
        mod = sb("mod", [P, 48 * 2])
        gain = sb("gain", [P, 2 * KT * 2])
        small = sb("small", [P, 64])
        eps, rms_sd, rms_r = small[:, 0:1], small[:, 1:6], small[:, 6:11]
        rms2_sd, rms2_r = small[:, 40:46], small[:, 46:52]
        nsink = small[:, 11:19]
        nmax, rsum, esink, tot, rinv = (small[:, 20 + 4 * i:24 + 4 * i] for i in range(5))
        scale_b = sb("scale_b", [P, KT])
        csilu = sb("csilu", [P, 4 * KT * 2])
        stat_sd = sb("stat_sd", [P, N_STAT * STAT_COLS])
        stat_r = sb("stat_r", [P, N_STAT * STAT_COLS])
        x = sb("x", [P, KT * T])
        stage = sb("stage", [P, RING, 1024])
        w_hi = sb("w_hi", [P, RING, 1024], F32R)
        w_lo = sb("w_lo", [P, RING, 1024], F32R)
        h_hi = sb("h_hi", [P, KT, T], F32R)
        h_lo = sb("h_lo", [P, KT, T], F32R)
        scr = sb("scr", [P, 10 * T])

        def scr_tile(i):
            return scr[:, i * T:(i + 1) * T]

        sq = [scr_tile(i) for i in (0, 1, 4)]
        acc = scr_tile(2)
        rbc = scr_tile(3)
        xn = [scr_tile(4), scr_tile(5)]
        h32 = [scr_tile(6), scr_tile(7)]
        sq2 = [scr[:, i * TH:(i + 1) * TH] for i in range(4)]
        s_neg = [scr[:, i * 512:(i + 1) * 512] for i in (0, 1)]
        e_sb = [scr[:, i * 512:(i + 1) * 512] for i in (2, 3)]
        p_sb = [scr[:, i * 512:(i + 1) * 512] for i in (4, 5)]
        pt_sb = [scr[:, i * 512:(i + 1) * 512] for i in (6, 7)]
        qsq = [scr[:, 4096 + i * T:4096 + (i + 1) * T] for i in range(3)]
        rope_s, rope_m = scr[:, 0:512], scr[:, 512:1024]
        r_wide = [scr[:, 1024 + i * T:1024 + (i + 1) * T] for i in range(4)]
        cb_t = scr[:, 3200:5248]
        cb_row = cb_t[0:1, :]
        ta, tb = scr_tile(0), scr_tile(1)
        ft = [scr_tile(4), scr_tile(5)]
        fp = [scr_tile(6), scr_tile(7)]
        

        with ExitStack() as s1:
            qk = sb("qk", [P, N_STAT, T], scope=s1)
            va = sb("va", [P, 5, P], scope=s1)
            vb = sb("vb", [P, 4, 512], scope=s1)
            vbh = sb("vbh", [64, 2, 512], scope=s1)
            cka = sb("cka", [P, P], scope=s1)
            cva = sb("cva", [P, P], scope=s1)
            ckb = sb("ckb", [P, 4, P], scope=s1)
            cvb = sb("cvb", [P, 512], scope=s1)
            cos = sb("cos", [P, LAT], scope=s1)
            sin = sb("sin", [P, LAT], scope=s1)
            amask = sb("amask", [P, 512], scope=s1)
            bb = sb("bb", [P, 4, 2, 384], scope=s1)
            vf = sb("vf", [P, 5, T], scope=s1)
            gates = [scr_tile(7), scr_tile(8), scr_tile(9)] + [vf[:, i, :] for i in range(5)]
            bb_flat = bb[:, :, :, :].rearrange("p a b c -> p (a b c)")
            cbc, junk = bb_flat[:, 0:2048], bb_flat[:, 2048:3072]
            ada1_st = ([qk[:, :, :].rearrange("p a t -> p (a t)")[:, i * 1024:(i + 1) * 1024] for i in range(8)]
                       + [vf[:, :, :].rearrange("p a t -> p (a t)")[:, i * 1024:(i + 1) * 1024] for i in range(2)])
        with ExitStack() as s2:
            y_hi = sb("y_hi", [P, KT, T], F32R, scope=s2)
            y_lo = sb("y_lo", [P, KT, T], F32R, scope=s2)
            m_hi = sb("m_hi", [P, KT, T], F32R, scope=s2)
            m_lo = sb("m_lo", [P, KT, T], F32R, scope=s2)

        ps = ctx.enter_context(nc.psum_tensor("ps", [P, 8, 512], F32))
        ident, heads1, one1 = cst[:, C_IDENT:C_IDENT + P], cst[:, C_HEADS:C_HEADS + 2], cst[:, C_ONE:C_ONE + 1]

        BC = [KA] + list(range(QB, QB + 4)) + list(range(KB, KB + 4))

        def slot_ps(s):
            return ps[:, 2 * s:2 * s + 2, 0:TH]

        def halves(tile):
            return tile.rearrange("p (a b) -> p a b", a=2)

        consts_in = sem("consts_in")
        c_in, cst_in = sem("c_in"), sem("cst_in")
        x_in = [sem(f"x_in{i}") for i in range(KT)]
        cache_in = sem("cache_in")
        stage_in = [sem(f"stage_in{i}") for i in range(RING)]
        bias_in = [sem(f"bias_in{i}") for i in range(4)]
        ada1_in = [sem(f"ada1_in{i}") for i in range(ADA1_SLOTS)]
        ada2_in = [sem(f"ada2_in{i}") for i in range(ADA2_SLOTS)]
        cbc_in = sem("cbc_in")
        xr_in = sem("xr_in")
        out_kv = sem("out_kv")
        out_y = sem("out_y")
        eps_set = sem("eps_set")
        c_tanh = sem("c_tanh")
        c_ready = sem("c_ready")
        ada_pe = sem("ada_pe")
        ada_dve = sem("ada_dve")
        mod1 = sem("mod1")
        mod2 = sem("mod2")
        sq_done = sem("sq_done")
        sum_done = sem("sum_done")
        x1_done, sum2_done, wo_half = sem("x1_done"), sem("sum2_done"), sem("wo_half")
        rms_ss, rms_sqrt, rms_rec, rms_bc, rbc_done = (sem(n) for n in
                                                       ("rms_ss", "rms_sqrt", "rms_rec", "rms_bc", "rbc_done"))
        xn_done, h32_done, hhi_done, h_ready = (sem(n) for n in ("xn_done", "h32_done", "hhi_done", "h_ready"))
        hi_done, lo_done, pe_unit = sem("hi_done"), sem("lo_done"), sem("pe_unit")
        act_read = sem("act_read")
        dve_read = sem("dve_read")
        qsq_done, ss_done, stat_sqrt, stat_ready = (sem(n) for n in ("qsq_done", "ss_done", "stat_sqrt", "stat_ready"))
        bc_done, bc_used, wide_done = sem("bc_done"), sem("bc_used"), sem("wide_done")
        rope_done = sem("rope_done")
        bb_zero = sem("bb_zero")
        vt_done, vt_used = sem("vt_done"), sem("vt_used")
        score_done, ttr_done, exp_done, norm_done, t_done, pt_done, pv_done, o_done = (
            sem(n) for n in ("score_done", "ttr_done", "exp_done", "norm_done", "t_done", "pt_done", "pv_done", "o_done"))
        yhi_done, y_ready = sem("yhi_done"), sem("y_ready")
        cb_tanh, cbc_ready, m32_done, mhi_done, m_ready = (sem(n) for n in ("cb_tanh", "cbc_ready", "m32_done", "mhi_done", "m_ready"))
        tanh_done, a32_done, ahi_done, a_ready = (sem(n) for n in ("tanh_done", "a32_done", "ahi_done", "a_ready"))
        y_done = sem("y_done")
        dve_own = sem("dve_own")

        BLOCKS = [(mixer, t, blk, hh) for mixer in "AB" for t in range(4) for blk in range(5) for hh in range(2)]
        N_RB = len(BLOCKS)
        HALF_RB = N_RB // 2

        def score_parts(mixer, t, blk, hh):
            r = slice(hh * HD, (hh + 1) * HD)
            if mixer == "A":
                k = qk[r, KA, :]
                if blk == 0:
                    return [(128, k[:, 0:CTX])]
                n = blk - 1
                last = min(n + 2, 4)
                parts = [(0, k[:, CTX + 128 * (n - 1):CTX + 128 * n])] if n else []
                return parts + [(128, cka[r, :]), (256, k[:, CTX + 128 * n:CTX + 128 * last])]
            k = qk[r, KB + t, :]
            if blk == 0:
                return [(0, k[:, 0:CTX])]
            c0, n = B_COL0[blk - 1] * ROWS, B_NCOL[blk - 1] * ROWS
            return [(0, ckb[r, t, :]), (128, k[:, CTX + c0:CTX + c0 + n])]

        def columns(mixer, t, blk, hh):
            parts = score_parts(mixer, t, blk, hh)
            return parts[0][0], parts[-1][0] + parts[-1][1].shape[1]

        def value_parts(mixer, t, blk, hh):
            if mixer == "A":
                c = slice(hh * HD, (hh + 1) * HD)
                if blk == 0:
                    return [(128, P, va[:, 0, c])]
                n = blk - 1
                out = [(0, P, va[:, n, c])] if n else []
                out += [(128, P, cva[:, c]), (256, P, va[:, n + 1, c])]
                return out + ([(384, P, va[:, n + 2, c])] if n < 3 else [])
            c = slice(t * P + hh * HD, t * P + (hh + 1) * HD)
            if blk == 0:
                return [(0, P, vb[:, 0, c])]
            ctxp = [(0, P, cvb[:, c])]
            if blk == 1:
                return ctxp + [(192, P, vb[:, 1, c]), (128, 64, vbh[:, 0, c])]
            if blk == 4:
                return ctxp + [(128, P, vb[:, 3, c]), (256, 64, vbh[:, 1, c])]
            return ctxp + [(128, P, vb[:, blk - 1, c]), (256, P, vb[:, blk, c])]

        GATE_FIRST = 3
        GATE_STEPS, due = [], 0
        for r in range(N_RB):
            due += N_GATE_ATT * KT - GATE_FIRST
            GATE_STEPS.append([])
            while due >= N_RB and GATE_FIRST + sum(map(len, GATE_STEPS)) < N_GATE_ATT * KT:
                step = divmod(GATE_FIRST + sum(map(len, GATE_STEPS)), KT)
                if step[1] == 0 and GATE_STEPS[-1]:
                    break
                GATE_STEPS[-1].append(step)
                due -= N_RB

        def gate_steps(r):
            return GATE_STEPS[r]

        SPLIT_HI_LATER, SPLIT_LO_LATER = 1, 2

        def ada2_sum(r):
            n = r // 2 - 1
            return (ADA2_QKV + n // 2, n % 2) if r % 2 == 0 and n >= 0 and n < 2 * (N_ADA2 - ADA2_QKV) else None

        def ada2_slot(a):
            return a % ADA2_SLOTS if a < ADA2_QKV else 3 + a % 2

        def ada2_unit(a):
            return x[:, ada2_slot(a) * 1024:(ada2_slot(a) + 1) * 1024]

        def ada2_arrived(a):
            return 16 * sum(ada2_slot(b) == ada2_slot(a) for b in range(a + 1))

        def gate_ended(r):
            return next((g for g, k in gate_steps(r) if k == KT - 1), None) if r >= 0 else None

        def grid_cols(tile):
            return tile[:, CTX:T].rearrange("p (c r) -> p r c", r=ROWS)

        def scale_bank(k):
            return 6 + k % 2 if k else 4

        X_BY_SP = (0, 2, 4, 5, 7)

        def load_x(eng, k):
            eng.dma_start(x[:, k * T:(k + 1) * T], x_t[:, k, :]).then_inc(x_in[k], 16)

        block = ctx.enter_context(nc.Block())

        @block.sync
        def _(sp):
            def load_unit(u, slot):
                sp.dma_start(stage[:, slot, :], w_main[u, :, :]).then_inc(stage_in[slot], 16)

            def load_pair(k):
                for m, src in enumerate((w_scale1[k, :, :], w_ada[k, :, :])):
                    slot = (2 * k + m) % ADA1_SLOTS
                    if k >= ADA1_SLOTS // 2:
                        sp.wait_ge((ada_pe, ada_dve)[m], k - ADA1_SLOTS // 2 + 1)
                    sp.dma_start(ada1_st[slot], src).then_inc(ada1_in[slot], 16)

            for k in X_BY_SP:
                load_x(sp, k)
            load_pair(0)
            for u in range(3):
                load_unit(u, u)
            for k in range(1, KT):
                if k == ADA1_SLOTS // 2:
                    load_unit(3, 3)
                    for dst, src in ((cos[:, :], consts[:, C_COS:C_COS + LAT]), (sin[:, :], consts[:, C_SIN:C_SIN + LAT]),
                                     (amask[:, :], consts[:, C_MASK:C_MASK + 512]), (cka[:, :], cache_ka), (cva[:, :], cache_va),
                                     (ckb[:, :, :], cache_kb), (cvb[:, :], cache_vb)):
                        sp.dma_start(dst, src).then_inc(cache_in, 16)
                load_pair(k)
            for u in range(RING, 2 * RING):
                sp.wait_ge(lo_done, u - RING + 1)
                load_unit(u, u % RING)

            def load_ada2(a):
                if a < ADA2_SLOTS:
                    sp.wait_ge(xn_done, KT)
                else:
                    sp.wait_ge(ada_dve, KT + (a - ADA2_SLOTS + 1 if a < ADA2_QKV else a - 1))
                sp.dma_start(ada2_unit(a), w_ada[KT + a, :, :]).then_inc(ada2_in[ada2_slot(a)], 16)

            def load_next(u):
                sp.wait_ge(lo_done, u - RING + 1)
                load_unit(u, u % RING)

            loaded = 0
            for u in range(N_QKV):
                load_next(u + 2 * RING)
                while loaded < min(sum(ADA2_OF[:u]) + ADA2_SLOTS, ADA2_QKV):
                    load_ada2(loaded)
                    loaded += 1
            sp.wait_ge(bc_used, 9)
            sp.dma_start(new_ka, qk[:, KA, 0:CTX]).then_inc(out_kv, 16)
            sp.dma_start(new_kb, qk[:, KB:KB + 4, 0:CTX]).then_inc(out_kv, 16)
            sp.wait_ge(act_read, N_QKV)
            sp.dma_start(new_va, vf[:, 0, 0:CTX]).then_inc(out_kv, 16)
            sp.dma_start(new_vb, vf[:, 1:5, 0:CTX]).then_inc(out_kv, 16)
            load_ada2(loaded)
            load_ada2(loaded + 1)
            for r in range(N_RB):
                if ada2_sum(r) and ada2_sum(r)[1] and ada2_sum(r)[0] + 2 < N_ADA2:
                    load_ada2(ada2_sum(r)[0] + 2)
                g = gate_ended(r - SPLIT_LO_LATER)
                if g is not None:
                    load_next(U_GATE + g + 2 * RING)
            late = sum(gate_ended(r) is not None for r in range(N_RB - SPLIT_LO_LATER, N_RB))
            for u in range(U_GATE + N_GATE_ATT - late + 2 * RING, U_WO):
                load_next(u)
            sp.wait_ge(y_ready, KT)
            sp.dma_start(x[:, :], x_t.rearrange("p k t -> p (k t)")).then_inc(xr_in, 16)
            n4 = (N_UNITS - U_WO) // RING
            with sp.Fori(0, n4) as i:
                for j in range(RING):
                    u = U_WO + j
                    sp.wait_ge(lo_done, i * RING + (u - RING + 1))
                    sp.dma_start(stage[:, u % RING, :], w_main[ds(i * RING + u, 1), :, :].rearrange("a p n -> p (a n)")
                                 ).then_inc(stage_in[u % RING], 16)
            for u in range(U_WO + n4 * RING, N_UNITS):
                load_next(u)
            for n in range(KT):
                sp.wait_ge(y_done, n + 1)
                sp.dma_start(y_t[:, n, :], x[:, n * T:(n + 1) * T]).then_inc(out_y, 16)
            sp.wait_ge(out_kv, 64)
            sp.wait_ge(out_y, 16 * KT)

        @block.gpsimd
        def _(pool):
            nc.gpsimd.memset(eps, RMS_EPS).then_inc(eps_set, 1)
            pool.wait_ge(stat_ready, 1)
            for i, tile in enumerate(BC):
                if i >= 4:
                    pool.wait_ge(bc_done, i - 3)
                r = stat_r[:, tile * STAT_COLS:(tile + 1) * STAT_COLS].unsqueeze(2).to_broadcast([P, STAT_COLS, HD])
                nc.gpsimd.tensor_copy(r_wide[i % 4].rearrange("p (c d) -> p c d", d=HD), r).then_inc(wide_done, 1)

            def split_lo(u, slot):
                pool.wait_ge(hi_done, u + 1)
                pool.wait_ge(lo_done, u)
                nc.gpsimd.tensor_tensor(w_lo[:, slot, :], stage[:, slot, :], w_hi[:, slot, :].bitcast(F32),
                                        ALU.subtract).then_inc(lo_done, 1)

            def sum_half(n):
                i = n
                pool.wait_ge(sq_done, KT + 4 + i + 1)
                pool.wait_ge(sum2_done, 4 + i)
                a = acc[:, TH:T]
                nc.gpsimd.tensor_tensor(a, a, sq2[i % 4], ALU.add).then_inc(sum2_done, 1)

            split_lo(U_FFN + 1, (U_FFN + 1) % RING)
            sum_half(4)
            split_lo(U_FFN + 2, (U_FFN + 2) % RING)
            sum_half(5)
            sum_half(6)

        @block.scalar
        def _(act):
            def split_hi(u, slot):
                use = (u - slot) * (16 // RING) + 16
                act.wait_ge(stage_in[slot], use)
                act.activation(w_hi[:, slot, :], stage[:, slot, :], ACT.Copy).then_inc(hi_done, 1)

            def h_tile(n, k, norm, cols):
                act.wait_ge(xn_done, n + 1)
                if n % KT >= 2:
                    act.wait_ge(h_ready, n - 1)
                shift = (SHIFT1, SHIFT2)[norm] * KT
                for kind, part in ((0, slice(0, CTX)), (1, slice(max(cols.start, CTX), cols.stop))):
                    if norm and not kind:
                        continue
                    g, s = (norm * KT + k) * 2 + kind, (shift + k) * 2 + kind
                    ins = act.activation(h32[k % 2][:, part], xn[k % 2][:, part], ACT.Identity,
                                         bias=mod[:, s:s + 1], scale=gain[:, g:g + 1])
                ins.then_inc(h32_done, 1)
                act.wait_ge(h32_done, n + 1)
                act.activation(h_hi[:, k, cols], h32[k % 2][:, cols], ACT.Copy).then_inc(hhi_done, 1)

            act.dma_start(csilu[:, 0:2 * KT], c_t).then_inc(c_in, 16)
            act.dma_start(cb_row, c_row).then_inc(cbc_in, 16)
            act.dma_start(cst[:, :], consts[:, 0:C_COS]).then_inc(cst_in, 16)
            act.dma_start(vec[:, :], vecs).then_inc(consts_in, 16)
            for k in range(KT):
                if k not in X_BY_SP:
                    load_x(act, k)
            act.wait_ge(c_in, 16)
            act.activation(csilu[:, 2 * KT:4 * KT], csilu[:, 0:2 * KT], ACT.Tanh, scale=0.5).then_inc(c_tanh, 1)
            for k in range(KT):
                act.wait_ge(x_in[k], 16)
                if k >= 3:
                    act.wait_ge(sum_done, k - 2)
                act.activation(sq[k % 3], x[:, k * T:(k + 1) * T], ACT.Square).then_inc(sq_done, 1)
            act.wait_ge(cbc_ready, 1)
            act.activation(cb_t.rearrange("p (a b) -> p a b", a=4), ps[:, 0:4, :], ACT.Tanh, scale=0.5).then_inc(cb_tanh, 1)
            act.wait_ge(eps_set, 1)
            act.activation(small[:, 52:53], eps, ACT.Sqrt)
            for u in range(3):
                split_hi(u, u)
            act.wait_ge(rms_ss, 1)
            act.activation(rms_sd, ps[:, 7, 0:5], ACT.Sqrt, bias=eps, scale=1.0 / D_MODEL).then_inc(rms_sqrt, 1)
            act.wait_ge(rms_bc, 1)
            act.activation(rbc[:, CTX:T], ps[:, 6, :], ACT.Copy)
            act.activation(rbc[:, 0:CTX], ps[:, 7, 0:CTX], ACT.Copy).then_inc(rbc_done, 1)
            for k in range(KT):
                act.wait_ge(mod1, k + 1)
                h_tile(k, k, 0, slice(0, T))
                if k == 5:
                    split_hi(3, 3)

            for u in range(N_QKV):
                slot = u % 3 if u < VB_T else u % 2
                act.wait_ge(pe_unit, u + 1)
                src = ps[:, 2 * slot:2 * slot + 2, :]
                if u < VA_T:
                    if u >= 3:
                        act.wait_ge(ss_done, u - 2)
                    act.activation(halves(qsq[u % 3]), src[:, :, 0:TH], ACT.Square).then_inc(qsq_done, 1)
                    col = V_GAIN + (0 if u < KA else 1 if u == KA else 2 if u < KB else 3)
                    fn, kw, dst = ACT.Identity, dict(scale=vec[:, col:col + 1]), qk[:, u, :]
                else:
                    fn, kw, dst = ACT.Copy, {}, vf[:, u - VA_T, :]
                if u <= KA or u == VA_T:
                    act.activation(halves(dst), src[:, :, 0:TH], fn, **kw).then_inc(act_read, 1)
                else:
                    act.activation(dst[:, 0:CTX], src[:, 0, 0:CTX], fn, **kw)
                    r0 = (TH - CTX) // GRID_W
                    act.activation(grid_cols(dst)[:, 0:r0, :],
                                   src[:, 0, CTX:TH].rearrange("p (r c) -> p r c", c=GRID_W), fn, **kw)
                    act.activation(grid_cols(dst)[:, r0:ROWS, :],
                                   src[:, 1, 0:TH].rearrange("p (r c) -> p r c", c=GRID_W), fn, **kw).then_inc(act_read, 1)
                split_hi(u + RING, u % RING)
                if u == VA_T:
                    act.wait_ge(ss_done, N_STAT)
                    act.activation(stat_sd[:, :], ps[:, 7, 0:N_STAT * STAT_COLS], ACT.Sqrt, bias=eps,
                                   scale=1.0 / HD).then_inc(stat_sqrt, 1)
            for i in range(5):
                act.wait_ge(vt_done, i + 1)
                b = 4 + 2 * (i % 2)
                if i == 0:
                    act.activation(va[:, 1:5, :], ps[:, b, :].rearrange("p (n d) -> p n d", n=4), ACT.Copy)
                    act.activation(va[:, 0, :], ps[:, b + 1, 0:P], ACT.Copy).then_inc(vt_used, 1)
                else:
                    act.activation(vb[:, :, (i - 1) * P:i * P], ps[:, b, :].rearrange("p (n d) -> p n d", n=4), ACT.Copy)
                    act.activation(vbh[:, :, (i - 1) * P:i * P],
                                   ps[0:64, b + 1, 0:2 * P].rearrange("p (n d) -> p n d", n=2), ACT.Copy).then_inc(vt_used, 1)

            def load_bias(t, j):
                act.dma_start(bb[:, j, :, 128:384], rpb[t, j, :, :, :]).then_inc(bias_in[j], 16)

            def take_gate(g):
                act.wait_ge(pe_unit, U_GATE + g + 1)
                if g == 3:
                    act.wait_ge(out_kv, 64)
                act.activation(halves(gates[g]), slot_ps(3), ACT.Tanh, scale=0.5).then_inc(act_read, 1)

            def exps(r):
                mixer, t, blk, hh = BLOCKS[r]
                lo, hi = columns(*BLOCKS[r])
                act.wait_ge(ttr_done, r + 1)
                if r >= 2:
                    act.wait_ge(norm_done, r - 1)
                ins = act.activation(e_sb[r % 2][:, lo:hi], s_neg[r % 2][:, lo:hi], ACT.Exp,
                                     bias=nmax[:, r % 4:r % 4 + 1], scale=-1.0, accum_out=rsum[:, r % 4:r % 4 + 1])
                if mixer == "A":
                    head = V_SINK + t + 4 * hh
                    ins = act.activation(esink[:, r % 4:r % 4 + 1], vec[:, head:head + 1], ACT.Exp,
                                         bias=nmax[:, r % 4:r % 4 + 1])
                ins.then_inc(exp_done, 1)
                t, j = divmod(r - HALF_RB - 3, 10)
                if t >= 0 and t < 3 and j in (0, 2, 4, 6):
                    load_bias(t + 1, j // 2)

            def copy_pt(r):
                act.wait_ge(t_done, r + 1)
                if r >= 2:
                    act.wait_ge(pv_done, r - 1)
                parts = value_parts(*BLOCKS[r])
                whole = sum(n == P for _, n, _ in parts) * P
                ins = act.activation(pt_sb[r % 2][:, 0:whole], ps[:, 2 + r % 2, 0:whole], ACT.Copy)
                if whole < len(parts) * P:
                    ins = act.activation(pt_sb[r % 2][0:64, whole:whole + P], ps[0:64, 2 + r % 2, whole:whole + P], ACT.Copy)
                ins.then_inc(pt_done, 1)

            def take_output(r):
                mixer, t, blk, hh = BLOCKS[r]
                p = r // 2
                act.wait_ge(pv_done, r + 1)
                tile = t if mixer == "A" else 4 + t
                y = x[:, tile * T:(tile + 1) * T]
                o = ps[:, 4 + p % 2, 0:P]
                if mixer == "A" or blk == 0:
                    ins = act.activation(y[:, blk * P:(blk + 1) * P], o, ACT.Copy)
                else:
                    w = P // ROWS
                    dst = y[:, CTX:T].rearrange("p (r c) -> p r c", r=ROWS)[:, :, (blk - 1) * w:blk * w]
                    ins = act.activation(dst, o.rearrange("p (c r) -> p r c", r=ROWS), ACT.Copy)
                ins.then_inc(o_done, 1)

            exps(0)
            exps(1)
            copy_pt(0)
            exps(2)
            for r in range(N_RB):
                if r + 1 < N_RB:
                    copy_pt(r + 1)
                if r + 3 < N_RB:
                    exps(r + 3)
                if r % 2:
                    take_output(r)
                if r == 31:
                    act.wait_ge(bb_zero, 1)
                    for j in range(4):
                        load_bias(0, j)
                if gate_ended(r) is not None:
                    take_gate(gate_ended(r))
                g = gate_ended(r - SPLIT_HI_LATER)
                if g is not None:
                    split_hi(U_GATE + g + RING, (U_GATE + g) % RING)

            for r in range(N_RB - SPLIT_HI_LATER, N_RB):
                g = gate_ended(r)
                if g is not None:
                    split_hi(U_GATE + g + RING, (U_GATE + g) % RING)

            act.wait_ge(out_kv, 64)
            for k in range(KT):
                act.wait_ge(o_done, N_RB // 2)
                act.activation(y_hi[:, k, :], x[:, k * T:(k + 1) * T], ACT.Copy).then_inc(yhi_done, 1)
            take_gate(N_GATE_ATT)
            split_hi(U_GATE + N_GATE_ATT + RING, (U_GATE + N_GATE_ATT) % RING)

            for n in range(KT):
                if n < 4:
                    u, merged = U_OUT + n, gates[2 * n]
                else:
                    u, merged = U_MERGE + 3 * (n - 4), ta
                    for m, dst in ((0, ta), (1, tb)):
                        act.wait_ge(pe_unit, u + 1)
                        if n > 4:
                            act.wait_ge(m_ready, n)
                        act.activation(halves(dst), slot_ps(m), ACT.Tanh, scale=0.5).then_inc(act_read, 1)
                        split_hi(u + RING, u % RING)
                        u += 1
                act.wait_ge(pe_unit, u + 1)
                split_hi(u + RING, u % RING)
                act.wait_ge(m32_done, n + 1)
                act.activation(m_hi[:, n, :], merged, ACT.Copy, scale=0.5).then_inc(mhi_done, 1)

            for j in range(4):
                act.wait_ge(pe_unit, U_WO + j + 1)
                split_hi(U_WO + j + RING, (U_WO + j) % RING)
                act.wait_ge(dve_read, KT + j + 1)
                if j >= 2:
                    act.wait_ge(sum2_done, j - 1)
                act.activation(scr_tile(j % 2), x[:, j * T:(j + 1) * T], ACT.Square).then_inc(sq_done, 1)

            def square_half(half, n):
                i = 4 * half + n - 4
                act.wait_ge(x1_done, i + 1)
                act.wait_ge(sum2_done, 4 + i - 3 if half else 2 + (i + 2) // 2)
                act.activation(sq2[i % 4], x[:, n * T + half * TH:n * T + (half + 1) * TH], ACT.Square).then_inc(sq_done, 1)

            def root(half):
                act.wait_ge(rms_ss, 2 + half)
                bank, c = half, 3 * half
                act.activation(rms2_sd[:, c:c + 2], ps[:, bank, 0:2], ACT.Sqrt, bias=eps, scale=1.0 / D_MODEL)
                act.activation(rms2_sd[0:TH - 2 * P, c + 2:c + 3], ps[0:TH - 2 * P, bank, 2:3], ACT.Sqrt,
                               bias=eps[0:TH - 2 * P, :], scale=1.0 / D_MODEL).then_inc(rms_sqrt, 1)

            def spread(half):
                act.wait_ge(rms_bc, 2 + half)
                act.activation(rbc[:, half * TH:(half + 1) * TH], ps[:, 2 + half, 0:TH], ACT.Copy).then_inc(rbc_done, 1)

            def split_ffn(u):
                act.wait_ge(pe_unit, u - RING + 1)
                split_hi(u, u % RING)

            def h_half(half, ks):
                for k in ks:
                    h_tile(KT * (1 + half) + k, k, 1, slice(half * TH, (half + 1) * TH))

            for n in range(4, KT):
                square_half(0, n)
            act.wait_ge(mod2, 1)
            act.activation(small[:, 52:53], eps, ACT.Sqrt)
            root(0)
            split_ffn(U_FFN)
            spread(0)
            h_half(0, (0, 1, 2))
            split_ffn(U_FFN + 1)
            square_half(1, 4)
            h_half(0, (3, 4))
            square_half(1, 5)
            h_half(0, (5,))
            split_ffn(U_FFN + 2)
            h_half(0, (6, 7))
            square_half(1, 6)
            square_half(1, 7)
            split_ffn(U_FFN + 3)
            root(1)
            spread(1)
            h_half(1, range(KT))

            u0, f0 = U_FFN, 0
            for part, nf in enumerate(FF_PARTS):
                with act.Fori(0, nf // 2) as i:
                    for j in range(2):
                        s = 2 * j
                        act.wait_ge(pe_unit, i * 4 + (u0 + 2 * j + 1))
                        act.activation(halves(ft[j]), slot_ps(s), ACT.Tanh, scale=0.5).then_inc(tanh_done, 1)
                        split_hi(i * 4 + (u0 + 2 * j + RING), (u0 + 2 * j) % RING)
                        act.wait_ge(pe_unit, i * 4 + (u0 + 2 * j + 2))
                        split_hi(i * 4 + (u0 + 2 * j + 1 + RING), (u0 + 2 * j + 1) % RING)
                        act.wait_ge(a32_done, i * 2 + (f0 + j + 1))
                        act.activation(y_hi[:, ds(i * 2 + j, 1), :].rearrange("p a t -> p (a t)"), fp[j],
                                       ACT.Copy).then_inc(ahi_done, 1)
                u0 += 2 * nf
                f0 += nf
                turns = 2 if part < 2 else 1
                with act.Fori(0, turns) as i:
                    for j in range(4):
                        act.wait_ge(pe_unit, i * 4 + (u0 + j + 1))
                        split_hi(i * 4 + (u0 + j + RING), (u0 + j) % RING)
                u0 += KT

        @block.vector
        def _(dve):
            own = Chain(dve, dve_own)

            def split_lo(u, slot):
                dve.wait_ge(hi_done, u + 1)
                dve.tensor_tensor(w_lo[:, slot, :], stage[:, slot, :], w_hi[:, slot, :].bitcast(F32),
                                  ALU.subtract).then_inc(lo_done, 1)

            def x_scaled(n, k, cols):
                dve.tensor_tensor(xn[k % 2][:, cols], x[:, k * T + cols.start:k * T + cols.stop], rbc[:, cols],
                                  ALU.mult).then_inc(xn_done, 1)

            def h_low(n, k, cols):
                dve.wait_ge(hhi_done, n + 1)
                dve.tensor_tensor(h_lo[:, k, cols], h32[k % 2][:, cols], h_hi[:, k, cols].bitcast(F32),
                                  ALU.subtract).then_inc(h_ready, 1)

            dve.wait_ge(c_tanh, 1)
            own.mark(dve.scalar_tensor_tensor(out=csilu[:, 2 * KT:4 * KT], in0=csilu[:, 2 * KT:4 * KT], scalar=1.0,
                                              in1=csilu[:, 0:2 * KT], op0=ALU.add, op1=ALU.mult))
            own.wait()
            dve.tensor_scalar(csilu[:, 2 * KT:4 * KT], csilu[:, 2 * KT:4 * KT], 0.5, None, ALU.mult).then_inc(c_ready, 1)
            dve.wait_ge(consts_in, 16)
            dve.tensor_scalar(nsink, vec[:, V_SINK:V_SINK + 8], -1.0, None, ALU.mult)
            bias1 = V_BADA + SCALE1 * KT
            own.mark(dve.tensor_scalar(scale_b[:, :], vec[:, bias1:bias1 + KT], 1.0, None, ALU.add))
            for k in range(1, KT):
                dve.wait_ge(sq_done, k + 1)
                if k == 1:
                    dve.tensor_tensor(acc, sq[0], sq[1], ALU.add).then_inc(sum_done, 2)
                else:
                    dve.wait_ge(sum_done, k)
                    dve.tensor_tensor(acc, acc, sq[k % 3], ALU.add).then_inc(sum_done, 1)
            dve.wait_ge(cb_tanh, 1)
            four = "p (a b) -> p a b"
            own.mark(dve.scalar_tensor_tensor(out=cbc.rearrange(four, a=4), in0=cb_t.rearrange(four, a=4), scalar=1.0,
                                              in1=ps[:, 0:4, :], op0=ALU.add, op1=ALU.mult))
            own.wait()

            def ada_sum(n, tile, unit, v):
                if n and not v:
                    dve.wait_ge(ada_dve, n)
                ins = dve.tensor_tensor_reduce(out=unit if v else junk, in0=unit, in1=cbc[:, v * 1024:(v + 1) * 1024],
                                               scale=0.5, scalar=vec[:, V_BADA + tile:V_BADA + tile + 1],
                                               op0=ALU.mult, op1=ALU.add, accum_out=mod[:, 2 * tile + v:2 * tile + v + 1])
                if v:
                    ins.then_inc(ada_dve, 1)

            def ada2_part(a, v):
                if not v:
                    dve.wait_ge(ada2_in[ada2_slot(a)], ada2_arrived(a))
                ada_sum(KT + a, 2 * KT + a, ada2_unit(a), v)

            whole = slice(0, T)

            def shift_sum(k):
                slot = (2 * k + 1) % ADA1_SLOTS
                dve.wait_ge(ada1_in[slot], 16 * (1 + 2 * k // ADA1_SLOTS))
                ada_sum(k, k, ada1_st[slot], 0)
                ada_sum(k, k, ada1_st[slot], 1)

            def gain_and_scaled(k):
                dve.wait_ge(ada_pe, k + 1)
                dve.tensor_scalar(gain[:, 2 * k:2 * k + 2], ps[:, scale_bank(k), 0:2], scale_b[:, k:k + 1],
                                  vec[:, V_GATTN + k:V_GATTN + k + 1], ALU.add, ALU.mult).then_inc(mod1, 1)
                x_scaled(k, k, whole)

            shift_sum(0)
            dve.wait_ge(rms_sqrt, 1)
            dve.reciprocal(rms_r, rms_sd).then_inc(rms_rec, 1)
            for u in range(3):
                split_lo(u, u)
            dve.wait_ge(rbc_done, 1)
            gain_and_scaled(0)
            h_low(0, 0, whole)
            for k in range(1, KT):
                shift_sum(k)
                if k > 1:
                    h_low(k - 1, k - 1, whole)
                gain_and_scaled(k)
            h_low(KT - 1, KT - 1, whole)
            split_lo(3, 3)

            def rope(tile):
                lat = qk[:, tile, CTX:T]
                own.mark(dve.stream_shuffle(rope_s, lat, [(i + 16) % 32 for i in range(32)]))
                own.wait()
                own.mark(dve.tensor_tensor(rope_m, rope_s, sin[:, :], ALU.mult))
                own.mark(dve.tensor_tensor(lat, lat, cos[:, :], ALU.mult))
                own.wait()
                dve.tensor_tensor(lat, lat, rope_m, ALU.add).then_inc(rope_done, 1)

            def use_broadcast(i, tile, m):
                dve.wait_ge(bc_done, 3 * (i // 3) + 3)
                dst = qk[:, tile, :]
                dve.tensor_tensor(dst[:, 0:CTX], dst[:, 0:CTX], ps[:, 7, m * P:(m + 1) * P], ALU.mult)
                if tile == KA:
                    ins = dve.tensor_tensor(dst[:, CTX:T], dst[:, CTX:T], ps[:, 4 + m, :], ALU.mult)
                else:
                    ins = dve.tensor_tensor(grid_cols(dst), grid_cols(dst),
                                            ps[:, 4 + m, :].rearrange("p (r c) -> p r c", c=GRID_W), ALU.mult)
                ins.then_inc(bc_used, 1)

            summed = 0
            for u in range(N_QKV):
                split_lo(u + RING, u % RING)
                if u < KA:
                    if u == 0:
                        dve.wait_ge(cache_in, 16 * 7)
                    dve.wait_ge(act_read, u + 1)
                    rope(u)
                if u == VA_T:
                    dve.wait_ge(stat_sqrt, 1)
                    own.mark(dve.reciprocal(stat_r[:, :], stat_sd[:, :]))
                    own.wait()
                    own.mark(dve.tensor_scalar(stat_r[:, 0:KA * STAT_COLS], stat_r[:, 0:KA * STAT_COLS], -SCALE, None, ALU.mult))
                    dve.tensor_scalar(stat_r[:, QB * STAT_COLS:KB * STAT_COLS], stat_r[:, QB * STAT_COLS:KB * STAT_COLS],
                                      SCALE, None, ALU.mult).then_inc(stat_ready, 1)
                if VB_T <= u < N_QKV - 1:
                    for m in range(3):
                        i = 3 * (u - VB_T) + m
                        use_broadcast(i, BC[i], m)
                        if i == 0:
                            dve.wait_ge(bc_used, 1)
                            rope(KA)
                for _ in range(ADA2_OF[u]):
                    ada2_part(summed, 0)
                    ada2_part(summed, 1)
                    summed += 1
            dve.wait_ge(bc_used, 9)

            def negate_scores(r):
                mixer, t, blk, hh = BLOCKS[r]
                lo, hi = columns(*BLOCKS[r])
                dve.wait_ge(score_done, r + 1)
                if mixer == "A":
                    col = (QA + t) * STAT_COLS + 2 * blk + hh
                    head = t + 4 * hh
                    add, scale, init = amask[:, lo:hi], stat_r[:, col:col + 1], nsink[:, head:head + 1]
                else:
                    if blk and not hh:
                        dve.wait_ge(bias_in[blk - 1], 16 * (t + 1))
                    add, scale, init = bb[:, max(blk - 1, 0), hh, lo:hi], -1.0, BIG
                dve.tensor_tensor_reduce(out=s_neg[r % 2][:, lo:hi], in0=ps[:, r % 2, lo:hi], in1=add, scale=scale,
                                         scalar=init, op0=ALU.add, op1=ALU.min,
                                         accum_out=nmax[:, r % 4:r % 4 + 1]).then_inc(ttr_done, 1)

            def normalise(r):
                mixer = BLOCKS[r][0]
                lo, hi = columns(*BLOCKS[r])
                q = r % 4
                dve.wait_ge(exp_done, r + 1)
                total = rsum[:, q:q + 1]
                if mixer == "A":
                    own.mark(dve.tensor_tensor(tot[:, q:q + 1], rsum[:, q:q + 1], esink[:, q:q + 1], ALU.add))
                    own.wait()
                    total = tot[:, q:q + 1]
                own.mark(dve.reciprocal(rinv[:, q:q + 1], total))
                own.wait()
                if r >= 2:
                    dve.wait_ge(t_done, r - 1)
                dve.tensor_scalar(p_sb[r % 2][:, lo:hi], e_sb[r % 2][:, lo:hi], rinv[:, q:q + 1], None,
                                  ALU.mult).then_inc(norm_done, 1)

            negate_scores(0)
            negate_scores(1)
            normalise(0)
            negate_scores(2)
            normalise(1)
            for r in range(N_RB):
                if r + 3 < N_RB:
                    negate_scores(r + 3)
                if r + 2 < N_RB:
                    normalise(r + 2)
                if ada2_sum(r):
                    ada2_part(*ada2_sum(r))
                    if ada2_sum(r) == (N_ADA2 - 1, 1):
                        dve.wait_ge(ada_dve, KT + N_ADA2)
                        dve.memset(bb[:, :, :, 0:128], 0.0).then_inc(bb_zero, 1)
                        for v in range(2):
                            at = 2 * KT * SCALE2 + v
                            ins = dve.scalar_tensor_tensor(out=gain[:, 16 + v:32:2], in0=mod[:, at:at + 2 * KT - 1:2],
                                                           scalar=1.0, in1=vec[:, V_GFFN:V_GFFN + KT], op0=ALU.add,
                                                           op1=ALU.mult)
                        ins.then_inc(mod2, 1)
                g = gate_ended(r - SPLIT_LO_LATER)
                if g is not None:
                    split_lo(U_GATE + g + RING, (U_GATE + g) % RING)
            for r in range(N_RB - SPLIT_LO_LATER, N_RB):
                g = gate_ended(r)
                if g is not None:
                    split_lo(U_GATE + g + RING, (U_GATE + g) % RING)
            for k in range(KT):
                dve.wait_ge(yhi_done, k + 1)
                dve.tensor_tensor(y_lo[:, k, :], x[:, k * T:(k + 1) * T], y_hi[:, k, :].bitcast(F32),
                                  ALU.subtract).then_inc(y_ready, 1)
            split_lo(U_GATE + N_GATE_ATT + RING, (U_GATE + N_GATE_ATT) % RING)

            for n in range(KT):
                if n < 4:
                    u, ga, gb, s = U_OUT + n, gates[2 * n], gates[2 * n + 1], (0, 2)[n % 2]
                    read = U_GATE + N_GATE
                else:
                    u, ga, gb, s = U_MERGE + 3 * (n - 4), ta, tb, 2
                    read = U_GATE + N_GATE + 2 * (n - 3)
                    for m in range(2):
                        split_lo(u + RING, u % RING)
                        u += 1
                dve.wait_ge(act_read, read)
                dve.wait_ge(pe_unit, u + 1)
                for dst, slot in ((ga, s), (gb, s + 1)):
                    ins = dve.scalar_tensor_tensor(out=halves(dst), in0=halves(dst), scalar=1.0, in1=slot_ps(slot),
                                                   op0=ALU.add, op1=ALU.mult)
                ins.then_inc(dve_read, 1)
                dve.wait_ge(dve_read, n + 1)
                dve.tensor_tensor(ga, ga, gb, ALU.add).then_inc(m32_done, 1)
                split_lo(u + RING, u % RING)
                dve.wait_ge(mhi_done, n + 1)
                dve.scalar_tensor_tensor(out=m_lo[:, n, :], in0=ga, scalar=0.5, in1=m_hi[:, n, :].bitcast(F32),
                                         op0=ALU.mult, op1=ALU.subtract).then_inc(m_ready, 1)

            def add_gated(n, slot, gate):
                g = (gate * KT + n) * 2
                for half, a, b, t0, kind in ((0, 0, CTX, 0, 0), (0, CTX, TH, CTX, 1), (1, 0, TH, TH, 1)):
                    dst = x[:, ds(n * T + t0, b - a)]
                    ins = dve.scalar_tensor_tensor(out=dst, in0=ps[:, 2 * slot + half, a:b], scalar=mod[:, ds(g + kind, 1)],
                                                   in1=dst, op0=ALU.mult, op1=ALU.add)
                return ins

            dve.wait_ge(xr_in, 16)
            for j in range(4):
                split_lo(U_WO + j + RING, (U_WO + j) % RING)
                dve.wait_ge(pe_unit, U_WO + j + 1)
                add_gated(j, j, GATE1).then_inc(dve_read, 1)
                dve.wait_ge(sq_done, KT + j + 1)
                if j == 1:
                    dve.tensor_tensor(acc, scr_tile(0), scr_tile(1), ALU.add).then_inc(sum2_done, 2)
                elif j > 1:
                    dve.wait_ge(sum2_done, j)
                    dve.tensor_tensor(acc, acc, scr_tile(j % 2), ALU.add).then_inc(sum2_done, 1)

            def add_half(half, n):
                slot = n - 4
                dve.wait_ge(*((pe_unit, U_WO + n + 1) if half else (wo_half, n - 3)))
                for t0, t1, kind in (((0, CTX, 0), (CTX, TH, 1)) if not half else ((0, TH, 1),)):
                    at = n * T + half * TH
                    g = (GATE1 * KT + n) * 2 + kind
                    dst = x[:, at + t0:at + t1]
                    ins = dve.scalar_tensor_tensor(out=dst, in0=ps[:, 2 * slot + half, t0:t1], scalar=mod[:, g:g + 1],
                                                   in1=dst, op0=ALU.mult, op1=ALU.add)
                ins.then_inc(x1_done, 1)

            def sum_half(half, n):
                i = 4 * half + n - 4
                dve.wait_ge(sq_done, KT + 4 + i + 1)
                dve.wait_ge(sum2_done, 4 + i)
                a = acc[:, half * TH:(half + 1) * TH]
                dve.tensor_tensor(a, a, sq2[i % 4], ALU.add).then_inc(sum2_done, 1)

            def inverse(half):
                dve.wait_ge(rms_sqrt, 2 + half)
                c = 3 * half
                dve.reciprocal(rms2_r[:, c:c + 2], rms2_sd[:, c:c + 2])
                dve.reciprocal(rms2_r[0:TH - 2 * P, c + 2:c + 3], rms2_sd[0:TH - 2 * P, c + 2:c + 3]).then_inc(rms_rec, 1)

            def h_half(half, ks):
                for k in ks:
                    n = KT * (1 + half) + k
                    if k < KT:
                        if half:
                            x_scaled(n, k, slice(TH, T))
                        else:
                            own.mark(dve.tensor_tensor(xn[k % 2][:, 0:TH], x[:, k * T:k * T + TH], rbc[:, 0:TH], ALU.mult))
                            g, s = 2 * (KT + k), 2 * (SHIFT2 * KT + k)
                            own.wait()
                            dve.tensor_scalar(h32[k % 2][:, 0:CTX], xn[k % 2][:, 0:CTX], gain[:, g:g + 1], mod[:, s:s + 1],
                                              ALU.mult, ALU.add).then_inc(xn_done, 1)
                    if k:
                        h_low(n - 1, k - 1, slice(half * TH, (half + 1) * TH))

            add_half(0, 4)
            for n in range(5, KT):
                add_half(0, n)
                sum_half(0, n - 1)
            sum_half(0, 7)
            inverse(0)
            add_half(1, 4)
            split_lo(U_FFN, U_FFN % RING)
            dve.wait_ge(rbc_done, 2)
            h_half(0, (0, 1, 2))
            add_half(1, 5)
            h_half(0, (3, 4, 5))
            add_half(1, 6)
            h_half(0, (6, 7, 8))
            add_half(1, 7)
            sum_half(1, 7)
            dve.wait_ge(lo_done, U_FFN + 3)
            split_lo(U_FFN + 3, (U_FFN + 3) % RING)
            inverse(1)
            dve.wait_ge(rbc_done, 3)
            h_half(1, range(KT + 1))

            u0, f0, read = U_FFN, 0, 2 * KT
            for part, nf in enumerate(FF_PARTS):
                with own.fori(nf // 2, 2) as i:
                    for j in range(2):
                        s = 2 * j
                        dve.wait_ge(tanh_done, i * 2 + (f0 + j + 1))
                        own.mark(dve.scalar_tensor_tensor(out=halves(ft[j]), in0=halves(ft[j]), scalar=1.0, in1=slot_ps(s),
                                                          op0=ALU.add, op1=ALU.mult))
                        split_lo(i * 4 + (u0 + 2 * j + RING), (u0 + 2 * j) % RING)
                        dve.wait_ge(pe_unit, i * 4 + (u0 + 2 * j + 2))
                        own.wait()
                        dve.scalar_tensor_tensor(out=halves(fp[j]), in0=slot_ps(s + 1), scalar=0.5, in1=halves(ft[j]),
                                                 op0=ALU.mult, op1=ALU.mult).then_inc(a32_done, 1)
                        split_lo(i * 4 + (u0 + 2 * j + 1 + RING), (u0 + 2 * j + 1) % RING)
                        dve.wait_ge(ahi_done, i * 2 + (f0 + j + 1))
                        dve.tensor_tensor(y_lo[:, ds(i * 2 + j, 1), :].rearrange("p a t -> p (a t)"), fp[j],
                                          y_hi[:, ds(i * 2 + j, 1), :].rearrange("p a t -> p (a t)").bitcast(F32),
                                          ALU.subtract).then_inc(a_ready, 1)
                u0 += 2 * nf
                f0 += nf
                last = part == len(FF_PARTS) - 1
                for turn in ([2] if not last else [1, 0]):
                    with dve.Fori(0, max(turn, 1)) as i:
                        n0 = 4 if turn == 0 else 0
                        for j in range(4):
                            if turn:
                                split_lo(i * 4 + (u0 + j + RING), (u0 + j) % RING)
                            dve.wait_ge(pe_unit, i * 4 + (u0 + n0 + j + 1))
                            add_gated(i * 4 + n0 + j, j, GATE2).then_inc(y_done if last else dve_read, 1)
                u0 += KT

        @block.tensor
        def _(pe):
            def k_products(out, w_slot, wk, r_hi, r_lo, rk, start, stop):
                w = slice(wk * P, (wk + 1) * P)
                for n, (wt, rt) in enumerate(((w_hi, r_hi), (w_hi, r_lo), (w_lo, r_hi))):
                    for half in range(2):
                        ins = pe.matmul(out[:, half, :], wt[:, w_slot, w], rt[:, rk, half * TH:(half + 1) * TH],
                                        start=start and n == 0, stop=stop and n == 2)
                return ins

            def unit(slot, w_slot, r_hi, r_lo, nk=KT, before=None):
                for k in range(nk):
                    if before:
                        before(k)
                    ins = k_products(slot_ps(slot), w_slot, k, r_hi, r_lo, k, k == 0, k == nk - 1)
                return ins

            def rms2_stats(half):
                pe.wait_ge(sum2_done, 4 * (half + 2))
                for c in range(3):
                    n = min(P, TH - c * P)
                    at = half * TH + c * P
                    ins = pe.matmul(ps[0:n, half, c:c + 1], acc[:, at:at + n], one1, start=True, stop=True)
                ins.then_inc(rms_ss, 1)

            def rms2_broadcast(half):
                pe.wait_ge(rms_rec, 2 + half)
                for c in range(3):
                    n = min(P, TH - c * P)
                    ins = pe.matmul(ps[:, 2 + half, c * P:c * P + n],
                                    rms2_r[0:n, 3 * half + c:3 * half + c + 1].to_broadcast([n, P]),
                                    ident[0:n, 0:n], start=True, stop=True)
                ins.then_inc(rms_bc, 1)

            def pair(slots, w_slots, r_hi, r_lo, nk, before):
                for k in range(nk):
                    before(k)
                    for s, w in zip(slots, w_slots):
                        ins = k_products(slot_ps(s), w, k, r_hi, r_lo, k, k == 0, k == nk - 1)
                        if k == nk - 1:
                            ins.then_inc(pe_unit, 1)

            def scale1(k):
                slot = 2 * k % ADA1_SLOTS
                pe.wait_ge(ada1_in[slot], 16 * (1 + 2 * k // ADA1_SLOTS))
                if k >= 2:
                    pe.wait_ge(mod1, k - 1)
                for j in range(KT):
                    ins = pe.matmul(ps[:, scale_bank(k), 0:2], ada1_st[slot][:, j * P:(j + 1) * P],
                                    csilu[:, 2 * KT + 2 * j:2 * KT + 2 * j + 2], start=j == 0, stop=j == KT - 1)
                ins.then_inc(ada_pe, 1)

            pe.wait_ge(cst_in, 16)
            pe.wait_ge(cbc_in, 16)
            for b in range(4):
                ins = pe.matmul(ps[:, b, :], one1[0:1, :].to_broadcast([1, P]), cb_row[:, b * 512:(b + 1) * 512],
                                start=True, stop=True)
            ins.then_inc(cbc_ready, 1)
            pe.wait_ge(c_ready, 1)
            scale1(0)
            pe.wait_ge(sum_done, KT)
            for c in range(5):
                ins = pe.matmul(ps[:, 7, c:c + 1], acc[:, c * P:(c + 1) * P], one1, start=True, stop=True)
            ins.then_inc(rms_ss, 1)
            pe.wait_ge(rms_rec, 1)
            for c in (1, 2, 3, 4, 0):
                out = ps[:, 7, 0:P] if c == 0 else ps[:, 6, (c - 1) * P:c * P]
                ins = pe.matmul(out, rms_r[:, c:c + 1].to_broadcast([P, P]), ident, start=True, stop=True)
            ins.then_inc(rms_bc, 1)

            pe.wait_ge(lo_done, 3)
            pe.wait_ge(rbc_done, 1)
            for k in range(KT):
                if k + 1 < KT:
                    scale1(k + 1)
                pe.wait_ge(h_ready, k + 1)
                for u in range(3):
                    ins = k_products(slot_ps(u), u, k, h_hi, h_lo, k, k == 0, k == KT - 1)
                    if k == KT - 1:
                        ins.then_inc(pe_unit, 1)

            def tile_stats(i):
                pe.wait_ge(qsq_done, i + 1)
                for c in range(5):
                    at = i * STAT_COLS + 2 * c
                    ins = pe.matmul(ps[:, 7, at:at + 2], qsq[i % 3][:, c * P:(c + 1) * P], heads1, start=True, stop=True)
                ins.then_inc(ss_done, 1)

            def broadcasts(rnd):
                pe.wait_ge(stat_ready, 1)
                if rnd:
                    pe.wait_ge(bc_used, 3 * rnd)
                else:
                    pe.wait_ge(act_read, VA_T - 1)
                for m in range(3):
                    i = 3 * rnd + m
                    pe.wait_ge(wide_done, i + 1)
                    for c in range(5):
                        out = ps[:, 7, m * P:(m + 1) * P] if c == 0 else ps[:, 4 + m, (c - 1) * P:c * P]
                        ins = pe.matmul(out, r_wide[i % 4][:, c * P:(c + 1) * P], ident, start=True, stop=True)
                    ins.then_inc(bc_done, 1)

            for u in range(3, N_QKV):
                slot = u % 3 if u < VB_T else u % 2
                pe.wait_ge(lo_done, u + 1)
                pe.wait_ge(act_read, u - 2 if u < VB_T else u - 1)
                unit(slot, u % RING, h_hi, h_lo).then_inc(pe_unit, 1)
                if u == 3:
                    pe.wait_ge(mod1, KT)
                    tile_stats(0)
                    tile_stats(1)
                if u - 1 < N_STAT:
                    tile_stats(u - 1)
                if VB_T <= u < N_QKV - 1:
                    broadcasts(u - VB_T)

            def scores(r):
                mixer, t, blk, hh = BLOCKS[r]
                if r >= 2:
                    pe.wait_ge(ttr_done, r - 1)
                rows = slice(hh * HD, (hh + 1) * HD)
                q = qk[rows, (QA if mixer == "A" else QB) + t, blk * P:(blk + 1) * P]
                for at, keys in score_parts(*BLOCKS[r]):
                    ins = pe.matmul(ps[:, r % 2, at:at + keys.shape[1]], q, keys, start=True, stop=True)
                ins.then_inc(score_done, 1)

            def transposes(r):
                pe.wait_ge(norm_done, r + 1)
                for c, (at, n, _) in enumerate(value_parts(*BLOCKS[r])):
                    ins = pe.transpose(ps[0:n, 2 + r % 2, c * P:(c + 1) * P], p_sb[r % 2][:, at:at + n], ident)
                ins.then_inc(t_done, 1)

            def outputs(r):
                mixer, t, blk, hh = BLOCKS[r]
                p = r // 2
                pe.wait_ge(pt_done, r + 1)
                if p >= 2 and not hh:
                    pe.wait_ge(o_done, p - 1)
                parts = value_parts(*BLOCKS[r])
                for c, (_, n, v) in enumerate(parts):
                    ins = pe.matmul(ps[hh * HD:(hh + 1) * HD, 4 + p % 2, 0:P], v, pt_sb[r % 2][0:n, c * P:(c + 1) * P],
                                    start=c == 0, stop=c == len(parts) - 1)
                ins.then_inc(pv_done, 1)

            def gate_step(g, k):
                if k == 0:
                    pe.wait_ge(lo_done, U_GATE + g + 1)
                    pe.wait_ge(act_read, U_GATE + g)
                ins = k_products(slot_ps(3), (U_GATE + g) % RING, k, h_hi, h_lo, k, k == 0, k == KT - 1)
                if k == KT - 1:
                    ins.then_inc(pe_unit, 1)

            pe.wait_ge(cache_in, 16 * 7)
            pe.wait_ge(rope_done, 5)
            pe.wait_ge(bc_used, 9)
            pe.wait_ge(act_read, N_QKV - 1)
            scores(0)
            scores(1)

            for i in range(5):
                pe.wait_ge(act_read, VA_T + i + 1)
                if i == 0:
                    pe.wait_ge(bc_used, 9)
                if i >= 2:
                    pe.wait_ge(vt_used, i - 1)
                b = 4 + 2 * (i % 2)
                src = vf[:, i, :]
                if i == 0:
                    for c in range(1, 5):
                        pe.transpose(ps[:, b, (c - 1) * P:c * P], src[:, c * P:(c + 1) * P], ident)
                    pe.transpose(ps[:, b + 1, 0:P], src[:, 0:CTX], ident).then_inc(vt_done, 1)
                else:
                    edge = 8 * ROWS
                    for c, at in enumerate((0, CTX + edge, CTX + edge + P, CTX + edge + 2 * P)):
                        pe.transpose(ps[:, b, c * P:(c + 1) * P], src[:, at:at + P], ident)
                    pe.transpose(ps[0:64, b + 1, 0:P], src[:, CTX:CTX + edge], ident)
                    pe.transpose(ps[0:64, b + 1, P:2 * P], src[:, T - edge:T], ident).then_inc(vt_done, 1)

            scores(2)
            pe.wait_ge(vt_used, 5)
            for k in range(GATE_FIRST):
                gate_step(0, k)
            transposes(0)
            for r in range(N_RB):
                if r + 3 < N_RB:
                    scores(r + 3)
                for g, k in gate_steps(r):
                    gate_step(g, k)
                if r + 1 < N_RB:
                    transposes(r + 1)
                outputs(r)

            pe.wait_ge(pt_done, N_RB)
            g = N_GATE_ATT
            pe.wait_ge(lo_done, U_GATE + g + 1)
            pe.wait_ge(act_read, U_GATE + g)
            unit(3, (U_GATE + g) % RING, h_hi, h_lo).then_inc(pe_unit, 1)
            pe.wait_ge(o_done, N_RB // 2)
            for n in range(KT):
                if n < 4:
                    u, s = U_OUT + n, (0, 2)[n % 2]
                    if n == 1:
                        pe.wait_ge(act_read, U_GATE + N_GATE)
                    if n >= 2:
                        pe.wait_ge(dve_read, n - 1)
                else:
                    u, s = U_MERGE + 3 * (n - 4), 2
                    for m in range(2):
                        pe.wait_ge(lo_done, u + 1)
                        if n == 4:
                            pe.wait_ge(dve_read, 3)
                        else:
                            pe.wait_ge(act_read, U_GATE + N_GATE + 2 * (n - 5) + m + 1)
                        unit(m, u % RING, h_hi, h_lo).then_inc(pe_unit, 1)
                        u += 1
                    pe.wait_ge(dve_read, n)
                pe.wait_ge(lo_done, u + 1)
                for k in range(KT):
                    if n == 0:
                        pe.wait_ge(y_ready, k + 1)
                    ins = k_products(slot_ps(s + k // 4), u % RING, k, y_hi, y_lo, k, k % 4 == 0, k % 4 == 3)
                ins.then_inc(pe_unit, 1)

            m_arrives = lambda k: pe.wait_ge(m_ready, k + 1)
            pe.wait_ge(act_read, U_GATE + N_GATE + 8)
            pe.wait_ge(lo_done, U_WO + 2)
            pair((0, 1), (U_WO % RING, (U_WO + 1) % RING), m_hi, m_lo, KT, m_arrives)
            pe.wait_ge(dve_read, KT)
            for j in (2, 3):
                pe.wait_ge(lo_done, U_WO + j + 1)
                unit(j, (U_WO + j) % RING, m_hi, m_lo).then_inc(pe_unit, 1)

            def half_unit(slot, half, u, r_hi, r_lo, before=None, middle=None):
                for k in range(KT):
                    if before:
                        before(k)
                    w = slice(k * P, (k + 1) * P)
                    for n, (wt, rt) in enumerate(((w_hi, r_hi), (w_hi, r_lo), (w_lo, r_hi))):
                        ins = pe.matmul(ps[:, 2 * slot + half, 0:TH], wt[:, u % RING, w],
                                        rt[:, k, half * TH:(half + 1) * TH],
                                        start=k == 0 and n == 0, stop=k == KT - 1 and n == 2)
                    if middle and k == 3:
                        middle()
                return ins

            for half in range(2):
                for j in range(4):
                    if not half:
                        pe.wait_ge(lo_done, U_WO + 4 + j + 1)
                        pe.wait_ge(dve_read, KT + j + 1)
                    middle = None
                    if half and j == 1:
                        middle = lambda: (pe.wait_ge(x1_done, 2), rms2_broadcast(0))
                    ins = half_unit(j, half, U_WO + 4 + j, m_hi, m_lo, middle=middle)
                    ins.then_inc(pe_unit if half else wo_half, 1)
                    if half and j == 0:
                        rms2_stats(0)
            u0, f0, read = U_FFN, 0, KT + 4
            for half in range(2):
                for j in range(4):
                    if not half:
                        pe.wait_ge(lo_done, U_FFN + j + 1)
                    before = (lambda k: pe.wait_ge(h_ready, KT * (1 + half) + k + 1)) if j == 0 else None
                    middle = (lambda: rms2_broadcast(1)) if not half and j == 1 else None
                    ins = half_unit(j, half, U_FFN + j, h_hi, h_lo, before, middle)
                    if half:
                        ins.then_inc(pe_unit, 1)
                    elif j == 0:
                        rms2_stats(1)
            for part, nf in enumerate(FF_PARTS):
                turns, skip = (nf // 2 - 1, 1) if part == 0 else (nf // 2, 0)
                with pe.Fori(0, turns) as i:
                    for j in range(2):
                        f = i * 2 + (2 * skip + j)
                        for m in range(2):
                            pe.wait_ge(lo_done, i * 4 + (u0 + 4 * skip + 2 * j + m + 1))
                            if m == 0:
                                if part == 0:
                                    pe.wait_ge(a32_done, f - 1)
                                else:
                                    pe.wait_ge(dve_read, read - 2 + 2 * j)
                                    pe.wait_ge(a32_done, i * 2 + (f0 + j - 1))
                            unit(2 * j + m, (u0 + 2 * j + m) % RING, h_hi, h_lo).then_inc(pe_unit, 1)
                u0 += 2 * nf
                f0 += nf
                last = part == len(FF_PARTS) - 1
                pe.wait_ge(lo_done, u0 + 2)
                pe.wait_ge(a32_done, f0 - 1)
                pair((0, 1), (u0 % RING, (u0 + 1) % RING), y_hi, y_lo, nf, lambda k: pe.wait_ge(a_ready, f0 - nf + k + 1))
                for n in range(2, KT):
                    pe.wait_ge(lo_done, u0 + n + 1)
                    if n < 4:
                        pe.wait_ge(a32_done, f0)
                    else:
                        pe.wait_ge(y_done if last else dve_read, (0 if last else read) + n - 3)
                    unit(n % 4, (u0 + n) % RING, y_hi, y_lo, nk=nf).then_inc(pe_unit, 1)
                u0 += KT
                read += KT



def _tiles(w):
    k, n = w.shape
    return np.ascontiguousarray(w.reshape(k // P, P, n // P, P).transpose(2, 1, 0, 3)).reshape(n // P, P, k)


def _padded(units):
    out = np.zeros((units.shape[0], P, 1024), units.dtype)
    out[:, :, :units.shape[2]] = units
    return out


def _main_units(w_in, w_out_a, w_out_b, w_o, w_gate, w_up, w_down):
    head_cols = np.arange(A_HEADS * HD).reshape(2, 4, HD).transpose(1, 0, 2).reshape(-1)
    win = _tiles(w_in)
    qa = _tiles(w_in[:, head_cols])
    woa, wob = _tiles(w_out_a[head_cols]), _tiles(w_out_b)
    units = [qa, win[4:5], win[6:10], win[10:14], win[5:6], win[14:18]]
    out = [np.concatenate([woa[n:n + 1], wob[n:n + 1]], axis=2) for n in range(KT)]
    gate_pairs = [win[t:t + 1] for n in range(KT) for t in (18 + n, 26 + n)]
    units += gate_pairs[:N_GATE] + out[:4]
    for n in range(4, KT):
        units += gate_pairs[2 * n:2 * n + 2] + [out[n]]
    units.append(_tiles(w_o))
    gate, up, f0 = _tiles(w_gate), _tiles(w_up), 0
    for nf in FF_PARTS:
        units.append(np.stack([gate[f0:f0 + nf], up[f0:f0 + nf]], axis=1).reshape(2 * nf, P, 1024))
        units.append(_padded(_tiles(w_down[f0 * P:(f0 + nf) * P])))
        f0 += nf
    return np.ascontiguousarray(np.concatenate(units, axis=0))


def _constants(dtype):
    out = np.zeros((P, N_CONST), dtype)
    tok = np.arange(LAT)
    half = HD // 4
    inv = (1.0 / (np.float32(10000.0) ** (np.arange(half, dtype=np.float32) / np.float32(half)))).astype(np.float32)
    for p in range(P):
        d = p % HD
        pos = (tok // GRID_W if d < HD // 2 else tok % GRID_W).astype(np.float32)
        ang = pos * inv[d % half]
        out[p, C_COS:C_COS + LAT] = np.cos(ang)
        out[p, C_SIN:C_SIN + LAT] = np.sin(ang) * (-1.0 if d % (2 * half) < half else 1.0)
    q, k = np.arange(P)[:, None], np.arange(P)[None, :]
    out[:, C_MASK:C_MASK + P] = np.where(k >= q, 0.0, NEG)
    out[:, C_MASK + 3 * P:C_MASK + 4 * P] = np.where(k <= q, 0.0, NEG)
    out[:, C_IDENT:C_IDENT + P] = np.eye(P)
    out[:, C_HEADS] = np.arange(P) < HD
    out[:, C_HEADS + 1] = np.arange(P) >= HD
    out[:, C_ONE] = 1.0
    return out


def _bias_layout(rpb):
    out = np.full((4, 4, P, 2, 256), NEG, rpb.dtype)
    for j in range(4):
        cq = 16 * j + np.arange(P) // ROWS
        rq = np.arange(P) % ROWS
        n = B_NCOL[j] * ROWS
        kc = B_COL0[j] + np.arange(n) // ROWS
        kr = np.arange(n) % ROWS
        first = np.clip(cq - NA_COLS // 2, 0, GRID_W - NA_COLS)
        inside = (kc[None] >= first[:, None]) & (kc[None] < first[:, None] + NA_COLS)
        dr = kr[None] - rq[:, None] + NA_ROWS - 1
        dc = np.clip(kc[None] - cq[:, None], -(NA_COLS - 1), NA_COLS - 1) + NA_COLS - 1
        for h in range(B_HEADS):
            out[h // 2, j, :, h % 2, :n][inside] = rpb[h][dr, dc][inside]
    return out


def kernel(x_prompt, x_sample, cache_a_k, cache_a_v, cache_b_k, cache_b_v, c, c_ctx, w_ada, b_ada, g_attn, w_in,
           q_norm_a, k_norm_a, q_norm_b, k_norm_b, sink_a, rpb_b, w_out_a, w_out_b, w_o, g_ffn, w_gate, w_up, w_down):
    import concourse.bacc as bacc
    from concourse.bass_utils import run_bass_kernel_spmd

    a = {n: np.asarray(v) for n, v in locals().items() if n not in ("bacc", "run_bass_kernel_spmd")}
    f = a["x_prompt"].dtype

    def by_tile(v):
        return v.reshape(-1, P).T

    tokens = np.concatenate([a["x_prompt"][0], a["x_sample"][0]], axis=0)
    cs = np.stack([a["c_ctx"], a["c"][0]], axis=0)
    ada = a["w_ada"][0]
    n1 = KT * P
    twice = lambda v: np.concatenate([v, v])[:, None]
    arrays = {
        "x_t": tokens.reshape(T, KT, P).transpose(2, 1, 0),
        "c_t": cs.reshape(2, KT, P).transpose(2, 1, 0).reshape(P, 2 * KT),
        "c_row": cs.reshape(1, -1),
        "w_scale1": _tiles(ada[:, n1:2 * n1]),
        "w_ada": np.concatenate([ada[:, :n1], ada[:, 2 * n1:]], axis=1).T.reshape(N_ADA2 + KT, P, D_MODEL),
        "w_main": _main_units(*(a[n][0] for n in ("w_in", "w_out_a", "w_out_b", "w_o", "w_gate", "w_up", "w_down"))),
        "vecs": np.concatenate([by_tile(a["b_ada"][0]), by_tile(a["g_attn"][0]), by_tile(a["g_ffn"][0])]
                               + [twice(a[n][0]) for n in ("q_norm_a", "k_norm_a", "q_norm_b", "k_norm_b")]
                               + [np.broadcast_to(a["sink_a"][0], (P, A_HEADS))], axis=1),
        "consts": _constants(f),
        "cache_ka": a["cache_a_k"][0, 0].reshape(CTX, P).T,
        "cache_va": a["cache_a_v"][0, 0].reshape(CTX, P),
        "cache_kb": a["cache_b_k"][0, 0].reshape(CTX, 4, P).transpose(2, 1, 0),
        "cache_vb": a["cache_b_v"][0, 0].reshape(CTX, 4 * P),
        "rpb": _bias_layout(a["rpb_b"][0]),
    }
    outs = {"y_t": (P, KT, T), "new_ka": (P, CTX), "new_va": (P, CTX), "new_kb": (P, 4, CTX), "new_vb": (P, 4, CTX)}
    nc = bacc.Bacc("TRN2", target_bir_lowering=False, num_devices=1, dynamic_dma_scratch_size=1024)
    args = []
    for name, v in arrays.items():
        arrays[name] = v = np.ascontiguousarray(v)
        args.append(nc.dram_tensor(name, v.shape, mybir.dt.from_np(v.dtype), kind="ExternalInput").ap())
    for name, shape in outs.items():
        args.append(nc.dram_tensor(name, shape, mybir.dt.from_np(f), kind="ExternalOutput").ap())
    hybrid_dit_program(nc, *args)
    r = run_bass_kernel_spmd(nc, [arrays], core_ids=[0]).results[0]

    y = r["y_t"].transpose(2, 1, 0).reshape(T, D_MODEL)

    def heads(v, n):
        return v.reshape(P, -1, CTX).transpose(2, 1, 0).reshape(1, 1, CTX, n, HD)

    return (y[None, :CTX], y[None, CTX:], heads(r["new_ka"], 2), heads(r["new_va"], 2),
            heads(r["new_kb"], B_HEADS), heads(r["new_vb"], B_HEADS))
```
